# Optimizing a Trainium2 kernel written in Bass

```python
import jax
import jax.numpy as jnp
from jax import lax
import numpy as np

D_MODEL = 1024
BATCH = 1
SEQ = 256
DEPTH = 2

D_FF = 2816
RWKV_HEADS = 8
RWKV_HEAD_DIM = 64
RWKV_WIDTH = RWKV_HEADS * RWKV_HEAD_DIM
RWKV_DECAY_RANK = 32
RWKV_A_RANK = 32
RWKV_GATE_RANK = 96
MLSTM_HEADS = 4
MLSTM_HEAD_DIM = 128
MLSTM_WIDTH = MLSTM_HEADS * MLSTM_HEAD_DIM
MLSTM_CONV = 4
MLSTM_CHUNK = 128
RWKV_COLS = 3 * RWKV_WIDTH + RWKV_DECAY_RANK + RWKV_A_RANK + RWKV_GATE_RANK
MLSTM_COLS = 4 * MLSTM_WIDTH + 2 * MLSTM_HEADS
GATE_COLS = 2 * D_MODEL
N_IN = RWKV_COLS + MLSTM_COLS + GATE_COLS
RMS_EPS = 1e-6
RWKV_GN_EPS = 64e-5
MLSTM_NORM_EPS = 1e-5
L2_EPS = 1e-12

kernel_name = 'hybrid_rwkv7_mlstm_macaron_adaln'

def rms_norm(x, g):
    xf = x.astype(jnp.float32)
    y = xf * lax.rsqrt(jnp.mean(xf * xf, axis=-1, keepdims=True) + RMS_EPS)
    return (y * g.astype(jnp.float32)).astype(x.dtype)

def modulate(h, shift, scale):
    return h * (1 + scale[:, None, :]) + shift[:, None, :]

def swiglu(h, w_in, w_out):
    gate, up = jnp.split(h @ w_in, 2, axis=-1)
    return (jax.nn.silu(gate) * up) @ w_out

def head_norm(y, eps):
    mu = jnp.mean(y, axis=-1, keepdims=True)
    yc = y - mu
    return yc * lax.rsqrt(jnp.mean(yc * yc, axis=-1, keepdims=True) + eps)

def causal_depthwise_conv(x, w, b):
    width, chans = w.shape
    y = lax.conv_general_dilated(x, w[:, None, :], window_strides=(1,), padding=[(width - 1, 0)],
                                 dimension_numbers=('NWC', 'WIO', 'NWC'), feature_group_count=chans)
    return y + b

def rwkv7_recurrence(r, w, k, v, a, b):
    bsz, _, heads, n = r.shape

    def step(s, inp):
        r_t, w_t, k_t, v_t, a_t, b_t = inp
        sa = jnp.einsum('bhvk,bhk->bhv', s, a_t)
        s = s * w_t[:, :, None, :] + sa[..., None] * b_t[:, :, None, :] + v_t[..., None] * k_t[:, :, None, :]
        return s, jnp.einsum('bhvk,bhk->bhv', s, r_t)

    xs = tuple(jnp.moveaxis(t, 1, 0) for t in (r, w, k, v, a, b))
    s0 = jnp.zeros((bsz, heads, n, n), jnp.float32)
    _, y = lax.scan(step, s0, xs)
    return jnp.moveaxis(y, 0, 1)

def rwkv7_branch(p, mu, w0, w_up, a0, a_up, g_up, k_k, k_a, r_k, ln_g, ln_b):
    bsz, t_len, _ = p.shape
    hd = (bsz, t_len, RWKV_HEADS, RWKV_HEAD_DIM)
    pf = p.astype(jnp.float32)
    prev = jnp.pad(pf, ((0, 0), (1, 0), (0, 0)))[:, :-1]
    pf = pf + (prev - pf) * mu
    o1 = RWKV_WIDTH
    o4 = 3 * o1 + RWKV_DECAY_RANK
    o5 = o4 + RWKV_A_RANK
    r, k, v, w_lo, a_lo, g_lo = jnp.split(pf, [o1, 2 * o1, 3 * o1, o4, o5], axis=-1)
    w = w0 + jnp.tanh(w_lo) @ w_up
    w = -jax.nn.softplus(-w) - 0.5
    decay = jnp.exp(-jnp.exp(w))
    a = jax.nn.sigmoid(a0 + a_lo @ a_up)
    g = jax.nn.sigmoid(g_lo) @ g_up
    kk = (k * k_k).reshape(hd)
    kk = kk / jnp.maximum(jnp.sqrt(jnp.sum(kk * kk, axis=-1, keepdims=True)), L2_EPS)
    k = k * (1 + (a - 1) * k_a)
    r, k, v, decay, a = (t.reshape(hd) for t in (r, k, v, decay, a))
    y = rwkv7_recurrence(r, decay, k, v, -kk, kk * a)
    y = head_norm(y, RWKV_GN_EPS).reshape(bsz, t_len, RWKV_WIDTH) * ln_g + ln_b
    bonus = (jnp.sum(r * k * r_k, axis=-1, keepdims=True) * v).reshape(bsz, t_len, RWKV_WIDTH)
    return (y + bonus) * g

def mlstm_branch(p, conv_w, conv_b, gate_b, ln_g):
    bsz, t_len, _ = p.shape
    nh, dh, blk = MLSTM_HEADS, MLSTM_HEAD_DIM, MLSTM_CHUNK
    nc = t_len // blk
    wd = MLSTM_WIDTH
    pf = p.astype(jnp.float32)
    qk, v, o, gates = jnp.split(pf, [2 * wd, 3 * wd, 4 * wd], axis=-1)
    qk = jax.nn.silu(causal_depthwise_conv(qk, conv_w.astype(jnp.float32), conv_b))
    q, k = jnp.split(qk, 2, axis=-1)
    i_pre, f_pre = jnp.split(gates + gate_b, 2, axis=-1)

    def chunks(t):
        t = t.reshape((bsz, nc, blk, nh) + t.shape[3:])
        return jnp.moveaxis(t, 3, 1)

    q = chunks(q.reshape(bsz, t_len, nh, dh)) * dh ** -0.5
    k = chunks(k.reshape(bsz, t_len, nh, dh))
    v = chunks(v.reshape(bsz, t_len, nh, dh))
    log_i = chunks(i_pre)
    log_f = jax.nn.log_sigmoid(chunks(f_pre))
    b = jnp.cumsum(log_f, axis=-1)
    b_end = b[..., -1]
    causal = jnp.tril(jnp.ones((blk, blk), dtype=bool))
    d = jnp.where(causal, b[..., :, None] - b[..., None, :] + log_i[..., None, :], -jnp.inf)
    g_end = b_end[..., None] - b + log_i

    def step(carry, inp):
        c_st, n_st, m_st = carry
        k_c, v_c, g_c, be = inp
        m_new = jnp.maximum(be + m_st, jnp.max(g_c, axis=-1))
        keep = jnp.exp(be + m_st - m_new)
        wgt = jnp.exp(g_c - m_new[..., None])
        c_new = keep[..., None, None] * c_st + jnp.einsum('bhl,bhld,bhle->bhde', wgt, k_c, v_c)
        n_new = keep[..., None] * n_st + jnp.einsum('bhl,bhld->bhd', wgt, k_c)
        return (c_new, n_new, m_new), (c_st, n_st, m_st)

    init = (jnp.zeros((bsz, nh, dh, dh), jnp.float32), jnp.zeros((bsz, nh, dh), jnp.float32),
            jnp.full((bsz, nh), -jnp.inf, jnp.float32))
    xs = (jnp.moveaxis(k, 2, 0), jnp.moveaxis(v, 2, 0), jnp.moveaxis(g_end, 2, 0), jnp.moveaxis(b_end, 2, 0))
    _, (c_prev, n_prev, m_prev) = lax.scan(step, init, xs)
    c_prev = jnp.moveaxis(c_prev, 0, 2)
    n_prev = jnp.moveaxis(n_prev, 0, 2)
    m_prev = jnp.moveaxis(m_prev, 0, 2)
    m_inter = b + m_prev[..., None]
    m_t = jnp.maximum(m_inter, jnp.max(d, axis=-1))
    scores = jnp.einsum('bhcld,bhcsd->bhcls', q, k) * jnp.exp(d - m_t[..., None])
    inter = jnp.exp(m_inter - m_t)
    num = jnp.einsum('bhcls,bhcse->bhcle', scores, v) + inter[..., None] * jnp.einsum('bhcld,bhcde->bhcle', q, c_prev)
    den = jnp.sum(scores, axis=-1) + inter * jnp.einsum('bhcld,bhcd->bhcl', q, n_prev)
    h = num / jnp.maximum(jnp.abs(den), jnp.exp(-m_t))[..., None]
    h = jnp.moveaxis(h, 1, 3).reshape(bsz, t_len, nh, dh)
    h = head_norm(h, MLSTM_NORM_EPS).reshape(bsz, t_len, wd) * ln_g
    return jax.nn.sigmoid(o) * h

def token_mixer(h, w_in, rwkv_mu, rwkv_w0, rwkv_w_up, rwkv_a0, rwkv_a_up, rwkv_g_up, rwkv_k_k, rwkv_k_a,
                rwkv_r_k, rwkv_ln_g, rwkv_ln_b, mlstm_conv_w, mlstm_conv_b, mlstm_gate_b, mlstm_ln_g,
                branch_w_rwkv, branch_w_mlstm, w_out):
    p = h @ w_in
    p_r, p_m, p_g = jnp.split(p, [RWKV_COLS, RWKV_COLS + MLSTM_COLS], axis=-1)
    y_r = rwkv7_branch(p_r, rwkv_mu, rwkv_w0, rwkv_w_up, rwkv_a0, rwkv_a_up, rwkv_g_up, rwkv_k_k, rwkv_k_a,
                       rwkv_r_k, rwkv_ln_g, rwkv_ln_b) @ branch_w_rwkv
    y_m = mlstm_branch(p_m, mlstm_conv_w, mlstm_conv_b, mlstm_gate_b, mlstm_ln_g) @ branch_w_mlstm
    g_r, g_m = jnp.split(jax.nn.sigmoid(p_g.astype(jnp.float32)), 2, axis=-1)
    return ((g_r * y_r + g_m * y_m) @ w_out).astype(h.dtype)

def setup_inputs(seed: int = 0) -> dict:
    key = jax.random.key(seed)
    ks = jax.random.split(key, 32)
    f32 = jnp.float32

    def nrm(k, shape, scale):
        return jax.random.normal(k, shape, f32) * scale

    dm, w, mw = D_MODEL, RWKV_WIDTH, MLSTM_WIDTH
    return {
        'x': nrm(ks[0], (BATCH, SEQ, dm), 1.0),
        'c': nrm(ks[1], (BATCH, dm), 1.0),
        'ada_w': nrm(ks[2], (DEPTH, dm, 9 * dm), 0.1 * dm ** -0.5),
        'ada_b': nrm(ks[3], (DEPTH, 9 * dm), 0.02),
        'norm_g': 1.0 + nrm(ks[4], (DEPTH, 3, dm), 0.02),
        'ffn_w_in': nrm(ks[5], (DEPTH, 2, dm, 2 * D_FF), dm ** -0.5),
        'ffn_w_out': nrm(ks[6], (DEPTH, 2, D_FF, dm), D_FF ** -0.5),
        'mix_w_in': nrm(ks[7], (DEPTH, dm, N_IN), dm ** -0.5),
        'rwkv_mu': jax.random.uniform(ks[8], (DEPTH, RWKV_COLS), f32, 0.1, 0.9),
        'rwkv_w0': jnp.linspace(-6.0, -1.0, w, dtype=f32)[None, :] + nrm(ks[9], (DEPTH, w), 0.1),
        'rwkv_w_up': nrm(ks[10], (DEPTH, RWKV_DECAY_RANK, w), 0.1 * RWKV_DECAY_RANK ** -0.5),
        'rwkv_a0': nrm(ks[11], (DEPTH, w), 0.1),
        'rwkv_a_up': nrm(ks[12], (DEPTH, RWKV_A_RANK, w), 0.5 * RWKV_A_RANK ** -0.5),
        'rwkv_g_up': nrm(ks[13], (DEPTH, RWKV_GATE_RANK, w), RWKV_GATE_RANK ** -0.5),
        'rwkv_k_k': 0.85 + nrm(ks[14], (DEPTH, w), 0.02),
        'rwkv_k_a': 1.0 + nrm(ks[15], (DEPTH, w), 0.02),
        'rwkv_r_k': nrm(ks[16], (DEPTH, RWKV_HEADS, RWKV_HEAD_DIM), 0.1),
        'rwkv_ln_g': 1.0 + nrm(ks[17], (DEPTH, w), 0.02),
        'rwkv_ln_b': nrm(ks[18], (DEPTH, w), 0.02),
        'mlstm_conv_w': nrm(ks[19], (DEPTH, MLSTM_CONV, 2 * mw), MLSTM_CONV ** -0.5),
        'mlstm_conv_b': nrm(ks[20], (DEPTH, 2 * mw), 0.02),
        'mlstm_gate_b': jnp.concatenate([
            nrm(ks[21], (DEPTH, MLSTM_HEADS), 0.1),
            jnp.linspace(3.0, 6.0, MLSTM_HEADS, dtype=f32)[None, :] + nrm(ks[22], (DEPTH, MLSTM_HEADS), 0.1)],
            axis=-1),
        'mlstm_ln_g': 1.0 + nrm(ks[23], (DEPTH, mw), 0.02),
        'branch_w_rwkv': nrm(ks[24], (DEPTH, w, dm), w ** -0.5),
        'branch_w_mlstm': nrm(ks[25], (DEPTH, mw, dm), mw ** -0.5),
        'mix_w_out': nrm(ks[26], (DEPTH, dm, dm), dm ** -0.5),
        'final_g': 1.0 + nrm(ks[27], (dm,), 0.02),
    }

def reference(x, c, ada_w, ada_b, norm_g, ffn_w_in, ffn_w_out, mix_w_in, rwkv_mu, rwkv_w0, rwkv_w_up,
              rwkv_a0, rwkv_a_up, rwkv_g_up, rwkv_k_k, rwkv_k_a, rwkv_r_k, rwkv_ln_g, rwkv_ln_b,
              mlstm_conv_w, mlstm_conv_b, mlstm_gate_b, mlstm_ln_g, branch_w_rwkv, branch_w_mlstm,
              mix_w_out, final_g):
    cond = jax.nn.silu(c)
    for l in range(DEPTH):
        mod = cond @ ada_w[l] + ada_b[l]
        sh0, sc0, gt0, sh1, sc1, gt1, sh2, sc2, gt2 = jnp.split(mod, 9, axis=-1)
        h = modulate(rms_norm(x, norm_g[l, 0]), sh0, sc0)
        x = x + (0.5 * (1 + gt0))[:, None, :] * swiglu(h, ffn_w_in[l, 0], ffn_w_out[l, 0])
        h = modulate(rms_norm(x, norm_g[l, 1]), sh1, sc1)
        x = x + (1 + gt1)[:, None, :] * token_mixer(
            h, mix_w_in[l], rwkv_mu[l], rwkv_w0[l], rwkv_w_up[l], rwkv_a0[l], rwkv_a_up[l], rwkv_g_up[l],
            rwkv_k_k[l], rwkv_k_a[l], rwkv_r_k[l], rwkv_ln_g[l], rwkv_ln_b[l], mlstm_conv_w[l], mlstm_conv_b[l],
            mlstm_gate_b[l], mlstm_ln_g[l], branch_w_rwkv[l], branch_w_mlstm[l], mix_w_out[l])
        h = modulate(rms_norm(x, norm_g[l, 2]), sh2, sc2)
        x = x + (0.5 * (1 + gt2))[:, None, :] * swiglu(h, ffn_w_in[l, 1], ffn_w_out[l, 1])
    return rms_norm(x, final_g)


_drawn_inputs = setup_inputs


def setup_inputs(seed=0):
    import zlib

    import numpy as np

    out = dict(_drawn_inputs(seed))
    spreads = {}
    factors = {'rwkv_w_up': 8.0,
     'rwkv_a0': 3.052,
     'rwkv_k_k': 8.0,
     'rwkv_k_a': 6.574,
     'rwkv_ln_g': 7.608,
     'rwkv_ln_b': 7.234,
     'mlstm_conv_b': 8.0,
     'mlstm_ln_g': 7.039,
     'final_g': 3.113}
    for name, (base, spread) in spreads.items():
        noise = np.random.default_rng([zlib.crc32(name.encode()), seed]).standard_normal(out[name].shape)
        drawn = base * np.exp(spread * noise) if base else spread * noise
        out[name] = jnp.asarray(drawn.astype(out[name].dtype))
    for name, factor in factors.items():
        out[name] = (out[name] * factor).astype(out[name].dtype)
    return out
```

```python
from contextlib import ExitStack

import numpy as np

import concourse.bass as bass
from concourse import mybir

F32 = mybir.dt.float32
ALU = mybir.AluOpType
ACT = mybir.ActivationFunctionType
AXX = mybir.AxisListType.X

P = 128
D = 1024
KT = D // P
T = 256
TT = T // P
DEPTH = 2
FF = 2816
NC = FF // P
SLOTS = 4
SLOT = 3 * D
ROUNDS = NC // SLOTS
TAIL = NC - ROUNDS * SLOTS

RW = 512
NH = 4
C_WA = 3 * RW
C_G = C_WA + 64
C_Q = C_G + 96
C_K = C_Q + 512
C_V = C_K + 512
C_O = C_V + 512
C_IF = C_O + 512
C_GR = C_IF + 8
C_GM = C_GR + D

PROJ = [
    [(0, 384)], [(384, 384)], [(768, 384)], [(1152, 384)],
    [(C_WA, 160), (C_IF, 8), (C_Q, 128)],
    [(C_Q + 128, 384)],
    [(C_K, 384)],
    [(C_K + 384, 128), (C_V, 256)],
    [(C_V + 256, 256), (C_O, 128)],
    [(C_O + 128, 384)],
]
N_PROJ = len(PROJ)
N_MERGE = KT
N_OUT = 4
N_MIX = N_PROJ + N_MERGE + N_OUT
USES = NC + N_MIX + NC
FILL = [3] * NC + [len(b) for b in PROJ] + [4] * N_MERGE + [1] * N_OUT + [3] * NC
SLOT_OF = [u % SLOTS for u in range(NC + N_MIX)] + [c % SLOTS for c in range(NC)]
assert (NC + N_MIX) % SLOTS == 0

ADA_PRE = 8
ADA_WINDOW = 12
ADA_LAYER = 3 * ADA_WINDOW

DECAY = float(np.exp(-0.5))
RMS_EPS = 1e-6
GN_EPS = 64e-5
ML_EPS = 1e-5
L2_EPS = 1e-12
NEG = -1e30

R_ADA, R_NORM, ROWS_A = 0, 72, 96
RB_MU, RB_MUWA, RB_MUG, RB_W0, RB_A0, RB_KK, RB_KA, RB_RK, RB_LNG, RB_LNB = 0, 12, 13, 14, 18, 22, 26, 30, 34, 38
RB_CW, RB_CB, RB_MLG, RB_BI, RB_BF, ROWS_B = 42, 74, 82, 86, 87, 88
N_PARAM_DMAS = 20


class Steps:

    def __init__(self, name, numbers, sem):
        self.name, self.sem = name, sem
        self.known = numbers.get(name)
        self.numbers = numbers
        self.parts = [{"": 0}]

    def step(self, label=None):
        part = self.parts[-1]
        part[""] += 1
        if label is not None:
            assert label not in part, label
            part[label] = part[""]
        return self.sem, 1

    def next_part(self):
        self.parts.append({"": 0})

    def close(self):
        self.numbers[self.name] = self.parts

    def _value(self, l, n):
        if self.known is None:
            return self.sem, 1
        pre = self.known[0][""]
        if l is None:
            return self.sem, n
        if isinstance(l, str):
            return self.sem, pre + DEPTH * self.known[1][""] + n
        return self.sem, l * self.known[1][""] + (pre + n)

    def at(self, l, label):
        if self.known is None:
            return self.sem, 1
        return self._value(l, self.known[0 if l is None else 2 if isinstance(l, str) else 1][label])

    def last(self, l):
        return self._value(l, self.parts[-1][""])


def trunk(nc, numbers, x_in, c_in, ada_w, ada_b, norm_g, ffn_w_in, ffn_w_out, mix_w_in, rwkv_mu, rwkv_w0,
          rwkv_w_up, rwkv_a0, rwkv_a_up, rwkv_g_up, rwkv_k_k, rwkv_k_a, rwkv_r_k, rwkv_ln_g, rwkv_ln_b,
          conv_w, conv_b, gate_b, mlstm_ln_g, branch_r, branch_m, w_out, final_g, out):
    with ExitStack() as ctx:
        def sb(name, shape):
            return ctx.enter_context(nc.sbuf_tensor(name, shape, F32))

        def sem(name):
            return ctx.enter_context(nc.semaphore(name))

        def view(flat, *shape):
            names = "abcd"[:len(shape)]
            return flat.rearrange("p (" + " ".join(names) + ") -> p " + " ".join(names),
                                  **dict(zip(names, shape)))

        x = sb("x", [P, TT, D])
        xn = sb("xn", [P, TT, D])
        hT = sb("hT", [P, KT, T])
        ring = sb("ring", [P, SLOTS, SLOT])
        ada_stage = sb("ada_stage", [P, 2, KT, 256])
        ada_sum = sb("ada_sum", [P, 3 * D])
        gate_row = sb("gate_row", [P, D])
        shift_c = sb("shift_c", [P, KT])
        scale_c = sb("scale_c", [P, KT])
        cond = sb("cond", [P, KT])
        ss = sb("ss", [P, TT])
        rstd = sb("rstd", [P, TT])
        rows_a = sb("rows_a", [P, P])
        rows_b = sb("rows_b", [P, P])
        par_a = sb("par_a", [P, P])
        par_b = sb("par_b", [P, P])
        one_m_ka = sb("one_m_ka", [P, 4])
        up_wa = sb("up_wa", [64, 2, RW])
        up_g = sb("up_g", [96, RW])
        ident = sb("ident", [P, P])
        ones = sb("ones", [P, T])
        headsum = sb("headsum", [P, P])
        ident2 = sb("ident2", [P, 64])
        mask_t = sb("mask_t", [P, 4, P])
        mask_n = sb("mask_n", [P, 3, P])
        neg_mask = sb("neg_mask", [P, P])
        reset = sb("reset", [P, T])
        eps = sb("eps", [P, 4])
        raw = sb("raw", [P, 12, T + 1])
        raw_wa = sb("raw_wa", [64, T + 1])
        raw_g = sb("raw_g", [96, T + 1])
        low_wa = sb("low_wa", [64, T])
        low_g = sb("low_g", [96, T])
        y_r = sb("y_r", [P, 4, T])
        y_m = sb("y_m", [P, 4, T])
        nle = sb("nle", [P, 4])
        pend = sb("pend", [P, 2, 4])
        stat = sb("stat", [P, 4, 16])
        cols_m = sb("cols_m", [P, 20])
        tiny = sb("tiny", [4, 4])
        arena = sb("arena", [P, 16128])
        taken = [0]

        def carve(*shape):
            size = int(np.prod(shape))
            flat = arena[:, taken[0]:taken[0] + size]
            taken[0] += size
            assert taken[0] <= 16128, taken[0]
            return view(flat, *shape)

        hid = carve(2, T)
        sil = carve(2, T)
        taken[0] = 0
        conv_in = carve(8, T + 3)
        v_aug = carve(TT, NH, 129)
        sig_o = carve(4, T)
        qk = carve(8, T)
        e_t = carve(8, P)
        wk = carve(4, P)
        c_aug = carve(NH, 129)
        q_in = carve(4, P)
        rows_m = carve(11, T)
        taken[0] = 0
        ar = carve(2, TT, 2, P)
        bt = carve(2, T)
        kt = carve(2, T)
        m_t = carve(8, 4, P)
        m_n = carve(3, 8, P)
        hats = carve(2, 2, T)
        v_tm = carve(2, TT, P)
        b_tm = carve(2, TT, P)
        k_tm = carve(2, TT, P)
        az = carve(8, P)
        p2_flat = carve(8 * P)
        p2t_flat = carve(8 * P)
        xt_flat = carve(8 * P)
        diag = carve(4, 64)
        p2, p2t, xt = (view(f, 8, P) for f in (p2_flat, p2t_flat, xt_flat))
        uz = p2
        qt = view(p2t_flat[:, 0:512], 4, P)
        gt_s = view(p2t_flat[:, 512:768], 4, 64)
        s_s = view(xt_flat[:, 0:256], 4, 64)
        h_s = view(xt_flat[:, 256:640], 6, 64)
        d_in, d_ex, d_neg, d_end = (view(p2_flat, 4, T)[:, n, :] for n in range(4))
        sw, aa, cum, cum_x = (view(p2t_flat, 4, T)[:, n, :] for n in range(4))
        kk, sq, bb_, kp = (view(xt_flat, 4, T)[:, n, :] for n in range(4))
        shift_tmp = view(xn[:, 0, 0:512], 2, T)
        y_tmp = view(arena[:, 1024:1536], 2, T)
        head_sq = arena[:, 12288:13312]
        branch_gates = view(arena[:, 0:1024], 2, 2, T)
        merged = view(xn[:, :, :].rearrange("p a b -> p (a b)"), KT, T)
        yn_r = xn[:, :, 0:512]
        yn_m = xn[:, :, 512:1024]

        ps = ctx.enter_context(nc.psum_tensor("ps", [P, 8, 512], F32))

        def quad(b):
            return view(ps[:, b, :], 4, P)

        def duo(b):
            return view(ps[:, b, :], 2, T)

        slot_full = [sem(f"slot_full{s}") for s in range(SLOTS)]
        slot_free = sem("slot_free")
        ada_full = [sem(f"ada_full{s}") for s in range(2)]
        ring_ada = [sem(f"ring_ada{s}") for s in range(SLOTS)]
        ada_done = sem("ada_done")
        small_full = sem("small_full")
        params_full = sem("params_full")
        stored = sem("stored")
        gu_ready = sem("gu_ready")
        sil_ready = sem("sil_ready")
        hid_ready = sem("hid_ready")
        PE = Steps("pe_done", numbers, sem("pe_done"))
        DV = Steps("dve_done", numbers, sem("dve_done"))
        AC = Steps("act_done", numbers, sem("act_done"))
        PO = Steps("pool_done", numbers, sem("pool_done"))

        def landed(l, use):
            s = SLOT_OF[use]
            mine = [16 * FILL[u] * (SLOT_OF[u] == s) for u in range(USES)]
            return slot_full[s], l * sum(mine) + sum(mine[:use + 1])

        def landed_chunk(l, half, j, i):
            base = half * (NC + N_MIX)
            s, value = landed(l, base + i)
            return s, value + j * (16 * FILL[base])

        back = []
        for u in range(USES):
            n = 1
            while SLOT_OF[(u - n) % USES] != SLOT_OF[u]:
                n += 1
            back.append(n)

        def freed(l, use):
            return slot_free, l * USES + (use - back[use] + 1 + SLOTS)

        def y_done(l, name):
            if name == "mixer":
                return PE.at(l, "mixer Y")
            use = NC - 1 if name == "half 0" else USES - 1
            return slot_free, l * USES + (use + 1 + SLOTS)

        block = ctx.enter_context(nc.Block())

        @block.sync
        def _(sp):
            def chunk(l, half, col, slot, need):
                sp.wait_ge(slot_free, need)
                win = ffn_w_in[bass.ds(l, 1), half, :, :].rearrange("a (k p) (g n) -> p (a k) g n", p=P, g=2)
                for g in range(2):
                    sp.dma_start(view(ring[:, slot, 0:2048], 8, 2, P)[:, :, g, :], win[:, :, g, bass.ds(col, P)])\
                      .then_inc(slot_full[slot], 16)
                sp.dma_start(view(ring[:, slot, 2048:3072], 1, D),
                             ffn_w_out[bass.ds(l, 1), half, bass.ds(col, P), :].rearrange("a p n -> p a n"))\
                  .then_inc(slot_full[slot], 16)

            def ffn(l, half):
                base = half * (NC + N_MIX)
                for i in range(SLOTS):
                    chunk(l, half, i * P, i, freed(l, base + i)[1])
                with sp.Fori(1, ROUNDS) as j:
                    for i in range(SLOTS):
                        chunk(l, half, j * (SLOTS * P) + i * P, i,
                              l * USES + j * SLOTS + (base + i - SLOTS + 1 + SLOTS))
                for c in range(ROUNDS * SLOTS, NC):
                    chunk(l, half, c * P, c % SLOTS, freed(l, base + c)[1])

            sp.dma_start(rows_a[0:8, :], c_in.rearrange("a (k p) -> (a k) p", p=P)).then_inc(small_full, 16)
            sp.dma_start(x[:, :, :], x_in.rearrange("b (t p) d -> p (b t) d", p=P)).then_inc(small_full, 16)
            for n in range(SLOTS):
                sp.dma_start(view(ring[:, n, 0:2048], 8, 256),
                             ada_w[0, :, 256 * (2 + n):256 * (3 + n)].rearrange("(k p) n -> p k n", p=P))\
                  .then_inc(ring_ada[n], 16)
            sp.wait_ge(ada_done, 8 * (2 + SLOTS))
            with sp.Fori(0, DEPTH) as l:
                ll = bass.ds(l, 1)
                ffn(l, 0)
                win = mix_w_in[ll, :, :].rearrange("a (k p) n -> p (a k) n", p=P)
                for b, pieces in enumerate(PROJ):
                    use = NC + b
                    slot, wide = SLOT_OF[use], sum(w for _, w in pieces)
                    sp.wait_ge(*freed(l, use))
                    dst = view(ring[:, slot, 0:8 * wide], 8, wide)
                    at = 0
                    for col, width in pieces:
                        sp.dma_start(dst[:, :, at:at + width], win[:, :, col:col + width])\
                          .then_inc(slot_full[slot], 16)
                        at += width
                for ct in range(KT):
                    use = NC + N_PROJ + ct
                    slot, cols = SLOT_OF[use], slice(ct * P, ct * P + P)
                    sp.wait_ge(*freed(l, use))
                    for n, (src, rows_) in enumerate((
                            (win[:, :, C_GR + ct * P:C_GR + ct * P + P], 8),
                            (win[:, :, C_GM + ct * P:C_GM + ct * P + P], 8),
                            (branch_r[ll, :, cols].rearrange("a (k p) n -> p (a k) n", p=P), 4),
                            (branch_m[ll, :, cols].rearrange("a (k p) n -> p (a k) n", p=P), 4))):
                        at = (0, 1024, 2048, 2560)[n]
                        sp.dma_start(view(ring[:, slot, at:at + rows_ * P], rows_, P), src)\
                          .then_inc(slot_full[slot], 16)
                for n in range(N_OUT):
                    use = NC + N_PROJ + N_MERGE + n
                    slot = SLOT_OF[use]
                    sp.wait_ge(*freed(l, use))
                    sp.dma_start(view(ring[:, slot, 0:2048], 2, D),
                                 w_out[ll, n * 256:n * 256 + 256, :].rearrange("a (k p) n -> p (a k) n", p=P))\
                      .then_inc(slot_full[slot], 16)
                ffn(l, 1)
            sp.wait_ge(*DV.at(DEPTH - 1, "x updated by half 1"))
            sp.dma_start(gate_row[:, :], final_g.rearrange("(a n) -> a n", a=1).broadcast_to([P, D]))\
              .then_inc(small_full, 16)
            for t in range(TT):
                sp.wait_ge(*DV.at("end", f"out {t}"))
                sp.dma_start(out[0, t * P:t * P + P, :], xn[:, t, :]).then_inc(stored, 16)
            sp.wait_ge(stored, TT * 16)

        @block.gpsimd
        def _(po):
            def fill(tile, value, label=None):
                if PO.last(None)[1]:
                    po.wait_ge(*PO.last(None))
                po.memset(tile, value).then_inc(*PO.step(label))

            def keep(tile, op, base, pattern, cm, other, label=None):
                po.wait_ge(*PO.last(None))
                po.affine_select(out=tile, in_=tile, compare_op=op, fill=other, base=base,
                                 pattern=pattern, channel_multiplier=cm).then_inc(*PO.step(label))

            def unit(layer, col, s):
                po.dma_start(ada_stage[:, s, :, :],
                             ada_w[layer, :, bass.ds(col, 256)].rearrange("a (k p) n -> p (a k) n", p=P))\
                  .then_inc(ada_full[s], 16)

            unit(slice(0, 1), 0, 0)
            unit(slice(0, 1), 256, 1)
            fill(rows_b[:, :], 0.0)
            po.memset(cols_m[:, :], 0.0).then_inc(slot_free, SLOTS)
            fill(ident[:, :], 0.0)
            keep(ident[:, :], ALU.not_equal, 0, [[-1, P]], 1, 1.0, "ident")
            fill(ones[:, :], 1.0)
            for n, value in enumerate((RMS_EPS, GN_EPS, ML_EPS)):
                fill(eps[:, n:n + 1], value, "eps" if n == 2 else None)
            for u in range(2 + SLOTS, ADA_PRE):
                po.wait_ge(ada_done, 8 * (u - 1 - SLOTS))
                unit(slice(0, 1), 256 * u, u % 2)
            fill(raw[:, :, 0:1], 0.0)
            fill(up_wa[0:32, 1, :], 0.0)
            fill(up_wa[32:64, 0, :], 0.0)
            fill(raw_wa[:, 0:1], 0.0)
            fill(raw_g[:, 0:1], 0.0)
            fill(reset[:, :], 1.0)
            keep(view(reset[:, :], 4, 64), ALU.is_gt, 0, [[0, 4], [1, 64]], 0, 0.0)
            fill(headsum[:, :], 1.0)
            keep(headsum[:, 64:128], ALU.is_ge, -64, [[0, 64]], 1, 0.0)
            keep(headsum[:, 0:64], ALU.is_ge, 63, [[0, 64]], -1, 0.0)
            fill(ident2[:, :], 0.0)
            keep(ident2[:, :], ALU.not_equal, 0, [[-1, 64]], 1, 1.0)
            keep(ident2[:, :], ALU.not_equal, -64, [[-1, 64]], 1, 1.0)
            fill(neg_mask[:, :], 0.0)
            keep(neg_mask[:, :], ALU.is_ge, 0, [[1, P]], -1, NEG)

            def diagonal_blocks(tile, size):
                v = view(tile, P // size, size)
                keep(v, ALU.is_ge, 0, [[-size, P // size], [0, size]], 1, 0.0)
                keep(v, ALU.is_ge, size - 1, [[size, P // size], [0, size]], -1, 0.0)

            for n, (size, first) in enumerate(((16, 1), (64, 0), (64, 1), (64, 0))):
                fill(mask_t[:, n, :], 1.0)
                keep(mask_t[:, n, :], ALU.is_ge, -first, [[1, P]], -1, 0.0)
                diagonal_blocks(mask_t[:, n, :], size)
            for n, size in enumerate((16, 32, 64)):
                fill(mask_n[:, n, :], 1.0)
                keep(mask_n[:, n, :], ALU.is_ge, -1, [[-1, P]], 1, 0.0)
                diagonal_blocks(mask_n[:, n, :], size)
            for n in (2, 1):
                po.wait_ge(*PO.last(None))
                po.tensor_tensor(mask_n[:, n, :], mask_n[:, n, :], mask_n[:, n - 1, :], ALU.subtract)\
                  .then_inc(*PO.step("constants" if n == 1 else None))
            PO.next_part()

            with po.Fori(0, DEPTH) as l:
                sibling = po.snap(l * -1 + 1)
                for first, pairs, layer, col in ((0, 14, l, 2 * D), (28, 4, sibling, 0)):
                    with po.Fori(0, pairs) as j:
                        for s in range(2):
                            po.wait_ge(ada_done, l * (8 * ADA_LAYER) + j * 16 + 8 * (ADA_PRE + first + s - 1))
                            unit(bass.ds(layer, 1), j * 512 + (col + 256 * s), s)
            PO.close()

        @block.scalar
        def _(ac):
            def act(out_, in_, func, label=None, **kw):
                nc.scalar.activation(out_, in_, func, **kw).then_inc(*AC.step(label))

            def root_mean(l, name):
                for t in range(TT):
                    act(xn[:, t, :], x[:, t, :], ACT.Square, accum_out=ss[:, t:t + 1])
                ac.wait_ge(*AC.last(l))
                act(ss[:, :], ss[:, :], ACT.Sqrt, name + " root", scale=1.0 / D, bias=eps[:, 0:1])

            def modulated(l, name):
                ac.wait_ge(*DV.at(l, name + " columns"))
                for k in (0, 1, 4, 5):
                    ac.wait_ge(*PE.at(l, name + f" turned {k // 2}"))
                    act(hT[:, k, :], duo(4 + k // 2)[:, k % 2, :], ACT.Identity,
                        name + f" hT {k // 2}" if k % 2 else None,
                        scale=scale_c[:, k:k + 1], bias=shift_c[:, k:k + 1])

            def ffn(l, half):
                def silu(n, i):
                    ac.wait_ge(gu_ready, n + 1)
                    ac.wait_ge(hid_ready, n + 1)
                    nc.scalar.activation(sil[:, i % 2, :], ps[:, 4 + i % 2, 0:256], ACT.Silu).then_inc(sil_ready, 1)

                with ac.Fori(0, ROUNDS) as j:
                    for i in range(SLOTS):
                        silu(l * (2 * NC) + j * SLOTS + (half * NC + i), i)
                for i in range(ROUNDS * SLOTS, NC):
                    silu(l * (2 * NC) + (half * NC + i), i)

            ac.wait_ge(*PE.at(None, "c columns"))
            act(cond[:, :], ps[:, 4, 0:8], ACT.Silu, "cond")
            AC.next_part()
            ac.wait_ge(*PO.at(None, "eps"))
            ac.wait_ge(small_full, 32)
            with ac.Fori(0, DEPTH) as l:
                def rows(src):
                    return src.rearrange("a (r p) -> (a r) p", p=P)
                ll = bass.ds(l, 1)
                params = (
                    (rows_a[R_ADA:R_ADA + 72, :], rows(ada_b[ll, :])),
                    (rows_a[R_NORM:R_NORM + 24, :], norm_g[ll, :, :].rearrange("a n (r p) -> (a n r) p", p=P)),
                    (rows_b[RB_MU:RB_MU + 12, :], rows(rwkv_mu[ll, 0:C_WA])),
                    (rows_b[RB_MUWA:RB_MUWA + 1, 0:64], rwkv_mu[ll, C_WA:C_G]),
                    (rows_b[RB_MUG:RB_MUG + 1, 0:96], rwkv_mu[ll, C_G:C_Q]),
                    (rows_b[RB_W0:RB_W0 + 4, :], rows(rwkv_w0[ll, :])),
                    (rows_b[RB_A0:RB_A0 + 4, :], rows(rwkv_a0[ll, :])),
                    (rows_b[RB_KK:RB_KK + 4, :], rows(rwkv_k_k[ll, :])),
                    (rows_b[RB_KA:RB_KA + 4, :], rows(rwkv_k_a[ll, :])),
                    (rows_b[RB_RK:RB_RK + 4, :], rwkv_r_k[ll, :, :].rearrange("a (r h) n -> (a r) (h n)", h=2)),
                    (rows_b[RB_LNG:RB_LNG + 4, :], rows(rwkv_ln_g[ll, :])),
                    (rows_b[RB_LNB:RB_LNB + 4, :], rows(rwkv_ln_b[ll, :])),
                    (rows_b[RB_CW:RB_CW + 32, :], conv_w[ll, :, :].rearrange("a w (r p) -> (a w r) p", p=P)),
                    (rows_b[RB_CB:RB_CB + 8, :], rows(conv_b[ll, :])),
                    (rows_b[RB_MLG:RB_MLG + 4, :], rows(mlstm_ln_g[ll, :])),
                    (rows_b[RB_BI:RB_BI + 1, 0:4], gate_b[ll, 0:4]),
                    (rows_b[RB_BF:RB_BF + 1, 0:4], gate_b[ll, 4:8]),
                    (up_wa[0:32, 0, :], rwkv_w_up[ll, :, :].rearrange("a r n -> (a r) n")),
                    (up_wa[32:64, 1, :], rwkv_a_up[ll, :, :].rearrange("a r n -> (a r) n")),
                    (up_g[:, :], rwkv_g_up[ll, :, :].rearrange("a r n -> (a r) n")),
                )
                assert len(params) == N_PARAM_DMAS
                for dst, src in params:
                    ac.dma_start(dst, src).then_inc(params_full, 16)
                ac.wait_ge(*PE.at(l, "params"))
                act(par_a[:, 0:ROWS_A], ps[:, 4, 0:ROWS_A], ACT.Copy)
                act(par_b[:, 0:ROWS_B], ps[:, 4, 128:128 + ROWS_B], ACT.Copy, "params")
                root_mean(l, "norm 0")
                modulated(l, "norm 0")
                ffn(l, 0)
                ac.wait_ge(*PO.at(None, "constants"))
                ac.wait_ge(*DV.at(l, "x updated by half 0"))
                root_mean(l, "norm 1")
                modulated(l, "norm 1")

                for b in range(6):
                    ac.wait_ge(*PE.at(l, f"proj {b}"))
                    act(raw[:, 2 * b:2 * b + 2, 1:T + 1], duo(b), ACT.Copy, f"proj {b}")
                ac.wait_ge(*PE.at(l, "low rank"))
                act(raw_wa[:, 1:T + 1], ps[0:64, 6, 0:256], ACT.Copy)
                act(raw_g[:, 1:T + 1], ps[0:96, 6, 256:512], ACT.Copy, "low rank")
                li, fp, fa, lf, b_, c_, m_, nm, en, wg, im = range(11)
                R = rows_m[0:4]
                ac.wait_ge(*PE.at(l, "i f"))
                act(R[:, li, :], ps[0:4, 7, 0:256], ACT.Identity, bias=par_b[0:4, RB_BI:RB_BI + 1])
                act(R[:, fp, :], ps[0:4, 7, 256:512], ACT.Identity, "i f", bias=par_b[0:4, RB_BF:RB_BF + 1])
                ac.wait_ge(*AC.last(l))
                act(R[:, fa, :], R[:, fp, :], ACT.Abs)
                ac.wait_ge(*AC.last(l))
                act(R[:, fa, :], R[:, fa, :], ACT.Exp, scale=-1.0)
                ac.wait_ge(*AC.last(l))
                act(R[:, fa, :], R[:, fa, :], ACT.Ln, "ln f", bias=1.0)
                for b in range(4):
                    ac.wait_ge(*PE.at(l, f"qk {b}"))
                    act(conv_in[:, 2 * b:2 * b + 2, 3:T + 3], duo(b), ACT.Copy, f"qk {b}")
                ac.wait_ge(*DV.at(l, "low rank shifted"))
                act(low_wa[0:32, :], low_wa[0:32, :], ACT.Tanh, "tanh")
                ac.wait_ge(*DV.at(l, "convolved"))
                act(qk[:, :, :], qk[:, :, :], ACT.Silu, "qk ready")
                act(low_g[:, :], low_g[:, :], ACT.Sigmoid, "low g")
                for b in range(2):
                    ac.wait_ge(*PE.at(l, f"o {b}"))
                    act(sig_o[:, 2 * b:2 * b + 2, :], duo(6 + b), ACT.Sigmoid, f"o {b}")

                ac.wait_ge(*DV.at(l, "m rows"))
                act(R[:, en, :], R[:, en, :], ACT.Exp, scale=-1.0)
                act(R[:, wg, 0:P], R[:, c_, 0:P], ACT.Exp, bias=tiny[:, 1:2])
                act(R[:, im, P:T], R[:, m_, P:T], ACT.Exp, "m exps", scale=-1.0, bias=tiny[:, 2:3])
                ac.wait_ge(*DV.at(l, "e args"))
                act(e_t[:, :, :], e_t[:, :, :], ACT.Exp, "e")
                ac.wait_ge(*PE.at(l, "k turned"))
                ac.wait_ge(*DV.at(l, "cols_m"))
                for h in range(NH):
                    act(wk[:, h, :], quad(5)[:, h, :], ACT.Copy, "wk" if h == 3 else None,
                        scale=cols_m[:, 16 + h:17 + h])
                for b, bank in ((0, 5), (1, 4)):
                    ac.wait_ge(*PE.at(l, f"state {b}"))
                    act(c_aug[:, 2 * b:2 * b + 2, :], duo(bank)[:, :, 0:129], ACT.Copy, f"state {b}")
                ac.wait_ge(*DV.at(l, "m variance"))
                act(stat[:, 1, 0:8], stat[:, 1, 0:8], ACT.Sqrt, "m deviation", scale=1.0 / P, bias=eps[:, 2:3])

                for g in range(2):
                    for q in range(2):
                        p = 2 * g + q
                        ac.wait_ge(*(DV.at(l, f"prep {p - 1}") if q else
                                     DV.at(l, "y 0" if g else "y_m")))
                        ac.wait_ge(*PE.at(l, f"up {p}"))
                        act(sw, ps[:, 4, 0:256], ACT.Sigmoid, bias=par_b[:, RB_W0 + p:RB_W0 + p + 1])
                        act(aa, ps[:, 4, 256:512], ACT.Sigmoid, f"sigmoids {p}",
                            bias=par_b[:, RB_A0 + p:RB_A0 + p + 1])
                        act(sq, raw[:, 4 + p, 1:T + 1], ACT.Square, f"kk squared {p}",
                            scale=par_b[:, RB_KK + p:RB_KK + p + 1])
                        ac.wait_ge(*PE.at(l, f"kk norm {p}"))
                        act(sq, ps[:, 5, 0:256], ACT.Sqrt, f"kk norm {p}")
                        ac.wait_ge(*DV.at(l, f"cum {p}"))
                        act(d_in, cum, ACT.Exp, scale=-DECAY)
                        act(d_ex, cum_x, ACT.Exp, scale=-DECAY)
                        act(d_neg, cum, ACT.Exp, scale=DECAY)
                        for c in range(4):
                            act(d_end[:, 64 * c:64 * c + 64], cum[:, 64 * c:64 * c + 64], ACT.Exp,
                                scale=DECAY, bias=nle[:, c:c + 1])
                        act(pend[:, q, :], nle[:, :], ACT.Exp, f"decays {p}")
                        ac.wait_ge(*PE.at(l, f"turned {p} 0"))
                        act(v_tm[:, q, :, :], view(ps[:, 0, 0:256], 2, P), ACT.Copy)
                        act(az[:, 4 * q:4 * q + 4, 0:64], view(ps[:, 0, 256:512], 4, 64), ACT.Copy, f"turned {p} 0")
                        ac.wait_ge(*PE.at(l, f"turned {p} 1"))
                        act(b_tm[:, q, :, :], view(ps[:, 1, 0:256], 2, P), ACT.Copy)
                        act(k_tm[:, q, :, :], view(ps[:, 1, 256:512], 2, P), ACT.Copy, f"turned {p} 1")
                    ac.wait_ge(*PE.at(l, f"z0 {g}"))
                    act(az[:, :, 64:128], view(ps[:, 6, :], 8, 64), ACT.Copy, f"z0 {g}")

                    def copy(label, dst, bank):
                        for n in range(2):
                            ac.wait_ge(*PE.at(l, f"{label} {g} {n}"))
                            act(dst(n), quad(3 * n + bank), ACT.Copy, f"{label} {g} {n}")
                    copy("p2t", lambda n: p2t[:, 4 * n:4 * n + 4, :], 1)
                    copy("p4t", lambda n: m_t[:, 4 * n:4 * n + 4, 0, :], 1)
                    copy("p8", lambda n: p2[:, 4 * n:4 * n + 4, :], 0)
                    copy("x32", lambda n: p2t[:, 4 * n:4 * n + 4, :], 0)
                    copy("x64", lambda n: p2t[:, 4 * n:4 * n + 4, :], 0)
                    copy("uz", lambda n: uz[:, 4 * n:4 * n + 4, :], 0)
                    ac.wait_ge(*PE.at(l, f"h {g}"))
                    h_c = h_s.rearrange("p (q c) n -> p c q n", q=2)
                    act(h_c[:, 0::2], view(ps[:, 4, 0:256], 2, 2, 64), ACT.Copy)
                    act(h_c[:, 1], view(ps[:, 5, 0:128], 2, 64), ACT.Copy, f"h {g}")

                ac.wait_ge(*DV.at(l, "r variance"))
                act(stat[:, 1, :], stat[:, 1, :], ACT.Sqrt, "r deviation", scale=1.0 / 64, bias=eps[:, 1:2])
                for ct in range(KT):
                    ac.wait_ge(*PE.at(l, f"gates {ct}"))
                    if ct >= 2:
                        ac.wait_ge(*DV.at(l, f"merge {ct - 2}"))
                    act(branch_gates[:, ct % 2], duo(4 + ct % 2), ACT.Sigmoid, f"gates {ct}")
                ac.wait_ge(*DV.at(l, "x updated by mixer"))
                root_mean(l, "norm 2")
                modulated(l, "norm 2")
                ffn(l, 1)
                ac.wait_ge(*DV.at(l, "x updated by half 1"))
                act(tiny[:, 3:4], tiny[:, 1:2], ACT.Copy)
            AC.next_part()
            root_mean("end", "final")
            AC.close()

        @block.vector
        def _(dv):
            V = nc.vector

            def link(l, ins, label=None):
                ins.then_inc(*DV.step(label))
                dv.wait_ge(*DV.last(l))

            def free(ins, label=None):
                ins.then_inc(*DV.step(label))

            def ada(before, u, ks, stage_full, col, stage=None):
                s = u % 2
                if stage is None:
                    stage = ada_stage[:, s]
                    if ks[0] == 0:
                        dv.wait_ge(ada_full[s], stage_full)
                dst = ada_sum[:, bass.ds(col, 256)]
                for k in ks:
                    if k == 0:
                        V.tensor_scalar(dst, stage[:, 0, :], cond[:, 0:1], None, ALU.mult)\
                         .then_inc(ada_done, 1)
                    else:
                        dv.wait_ge(ada_done, before + k)
                        V.scalar_tensor_tensor(dst, stage[:, k, :], cond[:, k:k + 1], dst,
                                               ALU.mult, ALU.add).then_inc(ada_done, 1)

            def ada_unit(l, window, u, ks=range(8)):
                n = ADA_PRE + window * ADA_WINDOW + u
                ada(l * (8 * ADA_LAYER) + 8 * n, n, ks, l * (8 * ADA_LAYER) + 16 * ((n - SLOTS) // 2 + 1), 256 * u)

            def norm(l, name, gain_rows, shift_rows, scale_rows):
                dv.wait_ge(*AC.at(l, name + " root"))
                link(l, V.reciprocal(rstd[:, :], ss[:, :]))
                for t in range(TT):
                    free(V.tensor_scalar(xn[:, t, :], x[:, t, :], rstd[:, t:t + 1], None, ALU.mult),
                         name + f" xn {t}")
                dv.wait_ge(*PE.at(l, name + " columns"))
                free(V.tensor_tensor(shift_c[:, :], ps[:, 3, 0:8], par_a[:, shift_rows:shift_rows + 8], ALU.add))
                link(l, V.tensor_tensor(scale_c[:, :], ps[:, 3, 8:16], par_a[:, scale_rows:scale_rows + 8], ALU.add))
                link(l, V.scalar_tensor_tensor(scale_c[:, :], scale_c[:, :], 1.0,
                                               par_a[:, gain_rows:gain_rows + 8], ALU.add, ALU.mult),
                     name + " columns")
                for k in (2, 3, 6, 7):
                    dv.wait_ge(*PE.at(l, name + f" turned {k // 2}"))
                    free(V.tensor_scalar(hT[:, k, :], duo(4 + k // 2)[:, k % 2, :], scale_c[:, k:k + 1],
                                         shift_c[:, k:k + 1], ALU.mult, ALU.add),
                         name + f" hT {k // 2}" if k % 2 else None)

            def residual(l, name, factor):
                for n in range(2):
                    dv.wait_ge(*PE.at(l, name + f" gate {n}"))
                    free(V.tensor_scalar(gate_row[:, n * 512:n * 512 + 512], ps[:, 6 + n, :], factor, factor,
                                         ALU.mult, ALU.add))
                dv.wait_ge(*y_done(l, name))
                dv.wait_ge(*DV.last(l))
                for t in range(TT):
                    for n in range(2):
                        cols = slice(n * 512, n * 512 + 512)
                        free(V.tensor_tensor(xn[:, t, cols], ps[:, 2 * t + n, :], gate_row[:, cols], ALU.mult),
                             name + " Y read" if t == n == 1 else None)
                dv.wait_ge(*DV.last(l))
                for t in range(TT):
                    free(V.tensor_tensor(x[:, t, :], x[:, t, :], xn[:, t, :], ALU.add),
                         "x updated by " + name if t else None)
                dv.wait_ge(*DV.last(l))

            def ffn(l, half):
                window = 2 * half

                base = half * (NC + N_MIX)

                def chunk(n, i, use):
                    dv.wait_ge(sil_ready, n + 1)
                    dv.wait_ge(slot_free, use - 2 + 1 + SLOTS)
                    V.tensor_tensor(hid[:, i % 2, :], sil[:, i % 2, :], ps[:, 4 + i % 2, 256:512], ALU.mult)\
                     .then_inc(hid_ready, 1)

                with dv.Fori(0, ROUNDS) as j:
                    for i in range(SLOTS):
                        chunk(l * (2 * NC) + j * SLOTS + (half * NC + i), i, l * USES + j * SLOTS + (base + i))
                        u = i // 2
                        n = ADA_PRE + window * ADA_WINDOW + u
                        ada(l * (8 * ADA_LAYER) + j * 16 + 8 * n, u, range(4 * (i % 2), 4 * (i % 2) + 4),
                            l * (8 * ADA_LAYER) + j * 16 + 16 * ((n - SLOTS) // 2 + 1), j * 512 + 256 * u)
                for i in range(ROUNDS * SLOTS, NC):
                    chunk(l * (2 * NC) + (half * NC + i), i, l * USES + (base + i))
                for u in range(2 * ROUNDS, ADA_WINDOW):
                    ada_unit(l, window, u)

            def head_norm(l, y4, groups, size, name):
                mean, var = stat[:, 0, 0:groups], stat[:, 1, 0:groups]

                def per_head(a):
                    return view(a, 2, groups // 2).unsqueeze(3).broadcast_to([P, 2, groups // 2, size])
                for t in range(2):
                    free(V.tensor_reduce(view(mean, 2, groups // 2)[:, t, :], y4[:, t], AXX, ALU.add))
                dv.wait_ge(*DV.last(l))
                link(l, V.tensor_scalar(mean, mean, 1.0 / size, None, ALU.mult))
                link(l, V.tensor_tensor(y4, y4, per_head(mean), ALU.subtract))
                sqv = head_sq[:, :].rearrange("p (a b c) -> p a b c", a=2, b=groups // 2)
                link(l, V.tensor_tensor(sqv, y4, y4, ALU.mult))
                for t in range(2):
                    free(V.tensor_reduce(view(var, 2, groups // 2)[:, t, :], sqv[:, t], AXX, ALU.add),
                         name + " variance" if t else None)
                dv.wait_ge(*AC.at(l, name + " deviation"))
                link(l, V.reciprocal(var, var))
                link(l, V.tensor_tensor(y4, y4, per_head(var), ALU.mult), name + " normed")

            dv.wait_ge(*AC.at(None, "cond"))
            for u in range(ADA_PRE):
                if 2 <= u < 2 + SLOTS:
                    dv.wait_ge(ring_ada[u - 2], 16)
                    ada(8 * u, u, range(8), None, D + 256 * u, view(ring[:, u - 2, 0:2048], 8, 256))
                else:
                    ada(8 * u, u, range(8), 16 if u < 2 else 32, D + 256 * u)
            V.memset(stat[:, :, :], 0.0).then_inc(hid_ready, 2)
            DV.next_part()
            dv.wait_ge(hid_ready, 2)
            dv.wait_ge(small_full, 32)
            with dv.Fori(0, DEPTH) as l:
                dv.wait_ge(*AC.at(l, "params"))
                link(l, V.tensor_scalar(one_m_ka[:, :], par_b[:, RB_KA:RB_KA + 4], -1.0, 1.0, ALU.mult, ALU.add))
                norm(l, "norm 0", R_NORM, R_ADA, R_ADA + 8)
                ffn(l, 0)
                residual(l, "half 0", 0.5)
                norm(l, "norm 1", R_NORM + 8, R_ADA + 24, R_ADA + 32)
                dv.wait_ge(*PO.at(None, "constants"))

                dv.wait_ge(*PE.at(l, "norm 1 columns"))
                for u in range(0, 6):
                    ada_unit(l, 1, u)
                free(V.memset(v_aug[:, :, :, 128:129], 1.0))
                link(l, V.memset(conv_in[:, :, 0:3], 0.0))

                def shift(cur, prev, mu, dst, label, scratch):
                    link(l, V.tensor_tensor(scratch, prev, cur, ALU.subtract))
                    link(l, V.scalar_tensor_tensor(dst, scratch, mu, cur, ALU.mult, ALU.add), label)
                for i in range(12):
                    if i % 2 == 0:
                        dv.wait_ge(*AC.at(l, f"proj {i // 2}"))
                    shift(raw[:, i, 1:T + 1], raw[:, i, 0:T], par_b[:, RB_MU + i:RB_MU + i + 1],
                          raw[:, i, 1:T + 1], f"shifted {i}", shift_tmp[:, i % 2, :])
                dv.wait_ge(*AC.at(l, "low rank"))
                shift(raw_wa[:, 1:T + 1], raw_wa[:, 0:T], par_b[0:64, RB_MUWA:RB_MUWA + 1], low_wa[:, :], None,
                      shift_tmp[0:64, 0, :])
                shift(raw_g[:, 1:T + 1], raw_g[:, 0:T], par_b[0:96, RB_MUG:RB_MUG + 1], low_g[:, :],
                      "low rank shifted", shift_tmp[0:96, 1, :])

                li, fp, fa, lf, b_, c_, m_, nm, en, wg, im = range(11)
                R = rows_m[0:4]
                dv.wait_ge(*AC.at(l, "ln f"))
                link(l, V.scalar_tensor_tensor(R[:, lf, :], R[:, fp, :], 0.0, R[:, fa, :], ALU.min, ALU.subtract))
                for c in range(2):
                    w = slice(c * P, c * P + P)
                    link(l, V.tensor_tensor_scan(R[:, b_, w], ones[0:4, w], R[:, lf, w], 0.0, ALU.mult, ALU.add))
                link(l, V.tensor_tensor(R[:, c_, :], R[:, li, :], R[:, b_, :], ALU.subtract))
                link(l, V.tensor_tensor_scan(R[:, m_, 0:P], ones[0:4, 0:P], R[:, c_, 0:P], -3e38, ALU.mult, ALU.max))
                free(V.tensor_scalar(tiny[:, 1:2], R[:, m_, P - 1:P], -1.0, None, ALU.mult))
                link(l, V.tensor_tensor(tiny[:, 0:1], R[:, m_, P - 1:P], R[:, b_, P - 1:P], ALU.add))
                free(V.tensor_copy(tiny[:, 2:3], tiny[:, 0:1]))
                link(l, V.tensor_tensor_scan(R[:, m_, P:T], ones[0:4, 0:P], R[:, c_, P:T], tiny[:, 0:1],
                                             ALU.mult, ALU.max))
                free(V.tensor_scalar(R[:, nm, :], R[:, m_, :], -1.0, None, ALU.mult))
                link(l, V.tensor_tensor(R[:, en, :], R[:, b_, :], R[:, m_, :], ALU.add), "m rows")

                for i in range(8):
                    if i % 2 == 0:
                        dv.wait_ge(*AC.at(l, f"qk {i // 2}"))

                    def tap(w):
                        return par_b[:, RB_CW + 8 * w + i:RB_CW + 8 * w + i + 1]
                    link(l, V.tensor_scalar(qk[:, i, :], conv_in[:, i, 3:T + 3], tap(3),
                                            par_b[:, RB_CB + i:RB_CB + i + 1], ALU.mult, ALU.add))
                    for w in range(3):
                        link(l, V.scalar_tensor_tensor(qk[:, i, :], conv_in[:, i, w:w + T], tap(w), qk[:, i, :],
                                                       ALU.mult, ALU.add),
                             "convolved" if i == 7 and w == 2 else None)
                for t in range(TT):
                    dv.wait_ge(*PE.at(l, f"v {t}"))
                    free(V.tensor_copy(v_aug[:, t, :, 0:128], quad(4 + t)), f"v {t}")

                dv.wait_ge(*PE.at(l, "m columns"))
                link(l, V.tensor_copy(cols_m[:, :], ps[:, 4, 0:20]), "cols_m")
                dv.wait_ge(*PE.at(l, "m spread"))
                for c in range(2):
                    for h in range(NH):
                        free(V.scalar_tensor_tensor(
                            e_t[:, 4 * c + h, :], duo(2 + h // 2)[:, h % 2, c * P:c * P + P],
                            cols_m[:, 4 * c + h:4 * c + h + 1], neg_mask[:, :], ALU.add, ALU.min),
                            "e args" if c == 1 and h == 3 else None)
                dv.wait_ge(*AC.at(l, "e"))
                scale = float(P) ** -0.5
                for c in range(2):
                    dv.wait_ge(*PE.at(l, f"scores {c}"))
                    free(V.scalar_tensor_tensor(e_t[:, 4 * c:4 * c + 4, :], quad(c), scale,
                                                e_t[:, 4 * c:4 * c + 4, :], ALU.mult, ALU.mult), f"weights {c}")
                dv.wait_ge(*PE.at(l, "inter spread"))
                free(V.scalar_tensor_tensor(q_in[:, :, :], quad(4), scale, qk[:, 0:4, P:T], ALU.mult, ALU.mult),
                     "q_in")
                dv.wait_ge(*PE.at(l, "num"))
                num = ps[:, 0:4, :].rearrange("p a (b c) -> p (a b) c", b=2)
                den, size = stat[:, 3, 0:8], stat[:, 2, 0:8]
                link(l, V.tensor_copy(den, num[:, :, 128:129].rearrange("p a b -> p (a b)")))
                link(l, V.scalar_tensor_tensor(size, den, -1.0, den, ALU.mult, ALU.max))
                link(l, V.tensor_tensor(size, size, cols_m[:, 8:16], ALU.max))
                link(l, V.reciprocal(stat[:, 2, 0:8], stat[:, 2, 0:8]))
                ym4 = yn_m.rearrange("p a (b c) -> p a b c", b=4)
                for c in range(2):
                    free(V.tensor_tensor(ym4[:, c], num[:, 4 * c:4 * c + 4, 0:128],
                                         stat[:, 2, 4 * c:4 * c + 4].unsqueeze(2).broadcast_to([P, 4, P]),
                                         ALU.mult), "num read" if c else None)
                dv.wait_ge(*DV.last(l))
                head_norm(l, ym4, 8, P, "m")
                for h in range(NH):
                    dv.wait_ge(*PE.at(l, f"y_m {h // 2}"))
                    free(V.scalar_tensor_tensor(y_m[:, h, :], duo(h // 2)[:, h % 2, :],
                                                par_b[:, RB_MLG + h:RB_MLG + h + 1], sig_o[:, h, :],
                                                ALU.mult, ALU.mult), "y_m" if h == 3 else None)

                for g in range(2):
                    for q in range(2):
                        p = 2 * g + q
                        r_, k_, v_ = (raw[:, 4 * n + p, 1:T + 1] for n in range(3))
                        dv.wait_ge(*AC.at(l, f"sigmoids {p}"))
                        link(l, V.tensor_tensor_scan(cum, reset[:, :], sw, 0.0, ALU.mult, ALU.add))
                        free(V.tensor_scalar(nle[:, :], view(cum, 4, 64)[:, :, 63], -DECAY, None, ALU.mult))
                        link(l, V.tensor_tensor(cum_x, cum, sw, ALU.subtract), f"cum {p}")
                        link(l, V.tensor_scalar(kp, aa, par_b[:, RB_KA + p:RB_KA + p + 1],
                                                one_m_ka[:, p:p + 1], ALU.mult, ALU.add))
                        link(l, V.tensor_tensor(kp, kp, k_, ALU.mult))
                        link(l, V.scalar_tensor_tensor(kk, r_, par_b[:, RB_RK + p:RB_RK + p + 1], kp,
                                                       ALU.mult, ALU.mult), f"bonus weights {p}")
                        dv.wait_ge(*PE.at(l, f"bonus {p}"))
                        free(V.tensor_tensor(y_r[:, p, :], ps[:, 7, 256:512], v_, ALU.mult), f"bonus {p}")
                        dv.wait_ge(*AC.at(l, f"kk norm {p}"))
                        link(l, V.tensor_scalar(sq, sq, L2_EPS, None, ALU.max))
                        link(l, V.reciprocal(sq, sq))
                        link(l, V.scalar_tensor_tensor(kk, k_, par_b[:, RB_KK + p:RB_KK + p + 1], sq,
                                                       ALU.mult, ALU.mult))
                        link(l, V.tensor_tensor(bb_, kk, aa, ALU.mult))
                        dv.wait_ge(*AC.at(l, f"decays {p}"))
                        free(V.scalar_tensor_tensor(ar[:, q, :, 0, :], view(kk, 2, P), -1.0, view(d_ex, 2, P),
                                                    ALU.mult, ALU.mult))
                        free(V.tensor_tensor(ar[:, q, :, 1, :], view(r_, 2, P), view(d_in, 2, P), ALU.mult),
                             f"a r {p}")
                        free(V.tensor_tensor(hats[:, q, 0, :], bb_, d_end, ALU.mult))
                        free(V.tensor_tensor(hats[:, q, 1, :], kp, d_end, ALU.mult), f"hats {p}")
                        free(V.tensor_tensor(bt[:, q, :], bb_, d_neg, ALU.mult))
                        free(V.tensor_tensor(kt[:, q, :], kp, d_neg, ALU.mult), f"prep {p}")
                    for i in range(8):
                        dv.wait_ge(*PE.at(l, f"m_t {g} {i}"))
                        free(V.tensor_tensor(m_t[:, i, :, :], quad(i % 4), mask_t[:, :, :], ALU.mult), f"m_t {g} {i}")
                    dv.wait_ge(*DV.last(l))
                    for n in range(2):
                        dv.wait_ge(*PE.at(l, f"m_n {g} {n}"))
                        four = slice(4 * n, 4 * n + 4)
                        for m in range(3):
                            free(V.tensor_tensor(m_n[:, m, n::2, :], quad(4 + n),
                                                 mask_n[:, m:m + 1, :].broadcast_to([P, 4, P]), ALU.mult),
                                 f"m_n {g} {n}" if m == 2 else None)
                        free(V.tensor_tensor(xt[:, four, :], m_t[:, four, 0, :],
                                             ident[:, :].unsqueeze(1).broadcast_to([P, 4, P]), ALU.add),
                             f"xt 1 {g} {n}")

                    def evac(label, n, dst, bank):
                        dv.wait_ge(*PE.at(l, f"{label} {g} {n}"))
                        free(V.tensor_copy(dst, quad(3 * n + bank)), f"{label} {g} {n}")

                    def grow(label, n):
                        dv.wait_ge(*PE.at(l, f"{label} {g} {n}"))
                        four = xt[:, 4 * n:4 * n + 4, :]
                        free(V.tensor_tensor(four, four, quad(3 * n + 2), ALU.add), f"{label} {g} {n}")
                    for n in range(2):
                        evac("p2", n, p2[:, 4 * n:4 * n + 4, :], 0)
                    for n in range(2):
                        evac("p4", n, m_n[:, 0, 4 * n:4 * n + 4, :], 0)
                        grow("xt 2", n)
                    for label in ("xt 4", "xt 8"):
                        for n in range(2):
                            grow(label, n)
                    for size in (32, 64):
                        for n in range(2):
                            evac(f"g{size}", n, p2[:, 4 * n:4 * n + 4, :], 1)
                        for n in range(2):
                            grow(f"xt {size}", n)
                    def by_chunk(a):
                        return a.rearrange("p (q c) n -> p c q n", q=2)
                    free(V.tensor_tensor(view(diag.rearrange("p a b -> p (a b)"), 2, 2, 64),
                                         ident2[:, :].unsqueeze(1).unsqueeze(1).broadcast_to([P, 2, 2, 64]),
                                         pend[:, :, 1:3].unsqueeze(3).broadcast_to([P, 2, 2, 64]), ALU.mult))
                    dv.wait_ge(*PE.at(l, f"qt {g}"))
                    free(V.tensor_tensor(view(p2t_flat[:, 0:512], 2, 2, P), view(ps[:, 1, :], 2, 2, P),
                                         ar[:, :, :, 1, :], ALU.add), f"qt {g}")
                    dv.wait_ge(*PE.at(l, f"gt {g}"))
                    dv.wait_ge(*DV.last(l))
                    free(V.tensor_tensor(by_chunk(gt_s), ps[:, 2:4, 0:128].rearrange("p c (q n) -> p c q n", q=2),
                                         by_chunk(diag), ALU.add), f"gt {g}")
                    dv.wait_ge(*AC.at(l, f"h {g}"))
                    h3, s2 = h_s.rearrange("p (q c) n -> p q c n", q=2), s_s.rearrange("p (q c) n -> p q c n", q=2)
                    for c in (1, 2):
                        dv.wait_ge(*PE.at(l, f"chain {g} {c}"))
                        free(V.tensor_tensor(s2[:, :, c - 1, :], view(ps[:, 6, 128 * (c - 1):128 * c], 2, 64),
                                             h3[:, :, c, :], ALU.add), f"chain {g} {c}")
                    dv.wait_ge(*PE.at(l, f"y {g}"))
                    y_g = yn_r[:, :, 256 * g:256 * g + 256].rearrange("p t (q h n) -> p t q h n", q=2, h=2)
                    free(V.tensor_copy(y_g[:, :, :, 0], view(ps[:, 0, 0:256], 2, 2, 64)))
                    link(l, V.tensor_copy(y_g[:, :, :, 1], view(ps[:, 7, 0:256], 2, 2, 64)), f"y {g}")

                head_norm(l, yn_r.rearrange("p a (b c) -> p a b c", b=8), 16, 64, "r")
                for p in range(4):
                    scratch = y_tmp[:, p % 2, :]
                    dv.wait_ge(*PE.at(l, f"y turned {p // 2}"))
                    link(l, V.tensor_scalar(scratch, duo(p // 2)[:, p % 2, :], par_b[:, RB_LNG + p:RB_LNG + p + 1],
                                            par_b[:, RB_LNB + p:RB_LNB + p + 1], ALU.mult, ALU.add))
                    link(l, V.tensor_tensor(scratch, scratch, y_r[:, p, :], ALU.add))
                    dv.wait_ge(*PE.at(l, f"g {p // 2}"))
                    free(V.tensor_tensor(y_r[:, p, :], scratch, duo(2 + p // 2)[:, p % 2, :], ALU.mult),
                         "y_r" if p == 3 else None)
                for ct in range(KT):
                    sg = branch_gates[:, ct % 2]
                    dv.wait_ge(*AC.at(l, f"gates {ct}"))
                    dv.wait_ge(*PE.at(l, f"branches {ct}"))
                    link(l, V.tensor_tensor(sg, sg, duo(6 + ct % 2), ALU.mult), f"merged {ct}")
                    link(l, V.tensor_tensor(merged[:, ct, :], sg[:, 0, :], sg[:, 1, :], ALU.add), f"merge {ct}")
                for u in range(6, ADA_WINDOW):
                    ada_unit(l, 1, u)
                residual(l, "mixer", 1.0)
                norm(l, "norm 2", R_NORM + 16, R_ADA + 48, R_ADA + 56)
                ffn(l, 1)
                residual(l, "half 1", 0.5)
            DV.next_part()
            dv.wait_ge(*AC.at("end", "final root"))
            link("end", V.reciprocal(rstd[:, :], ss[:, :]))
            dv.wait_ge(small_full, 48)
            for t in range(TT):
                free(V.scalar_tensor_tensor(xn[:, t, :], x[:, t, :], rstd[:, t:t + 1], gate_row[:, :],
                                            ALU.mult, ALU.mult), f"out {t}")
            DV.close()

        @block.tensor
        def _(pe):
            def mm(out_, lhsT, rhs, start=True, stop=True, **kw):
                return nc.tensor.matmul(out_, lhsT, rhs, start=start, stop=stop, **kw)

            def turn(out_, in_):
                n = in_.shape[0]
                return nc.tensor.transpose(out_, in_, ident[0:n, 0:n])

            def columns(l, name):
                for n in range(16):
                    last = mm(ps[:, 3, n:n + 1], ada_sum[:, D + n * P:D + n * P + P], ones[:, 0:1])
                last.then_inc(*PE.step(name + " columns"))

            def gate(l, name, rows_, owed=None):
                for n in range(2):
                    first = mm(ps[:, 6 + n, :], ones[:, 0:P], ada_sum[:, n * 512:n * 512 + 512])
                    if n == 0 and owed is not None:
                        first.then_inc(slot_free, 1)
                    for r in range(4):
                        row = R_ADA + rows_ + 4 * n + r
                        last = mm(ps[:, 6 + n, r * P:r * P + P], ident[0:ROWS_A, row:row + 1].broadcast_to([ROWS_A, P]),
                                  rows_a[0:ROWS_A, :], start=False, skip_group_check=True)
                    last.then_inc(*PE.step(name + f" gate {n}"))

            def turned(l, name):
                for k2 in range(4):
                    for k in (2 * k2, 2 * k2 + 1):
                        for t in range(TT):
                            pe.wait_ge(*DV.at(l, name + f" xn {t}"))
                            last = turn(duo(4 + k2)[:, k % 2, t * P:t * P + P], xn[:, t, k * P:k * P + P])
                    last.then_inc(*PE.step(name + f" turned {k2}"))

            def ffn(l, half, name):
                use0 = half * (NC + N_MIX)

                def up(n, i, full):
                    w = view(ring[:, i % SLOTS, 0:2048], 8, 2, P)
                    pe.wait_ge(*full)
                    pe.wait_ge(hid_ready, n + 1)
                    for g in range(2):
                        for k in range(KT):
                            last = mm(duo(4 + i % 2)[:, g, :], w[:, k, g, :], hT[:, k, :], start=(k == 0),
                                      stop=(k == KT - 1))
                    last.then_inc(gu_ready, 1)

                def down(n, i, first, over):
                    pe.wait_ge(hid_ready, n + 3)
                    for t in range(TT):
                        for m in range(2):
                            last = mm(ps[:, 2 * t + m, :], hid[:, i % 2, t * P:t * P + P],
                                      ring[:, i % SLOTS, 2048 + m * 512:2560 + m * 512], start=first, stop=over)
                    last.then_inc(slot_free, 1)

                n0 = half * NC
                up(l * (2 * NC) + n0, 0, landed(l, use0))
                up(l * (2 * NC) + (n0 + 1), 1, landed(l, use0 + 1))
                down(l * (2 * NC) + n0, 0, True, False)
                with pe.Fori(0, ROUNDS - 1) as j:
                    for i in range(1, SLOTS + 1):
                        s, value = landed(l, use0 + i + 1)
                        up(l * (2 * NC) + j * SLOTS + (n0 + i + 1), i + 1, (s, value + j * (16 * FILL[use0])))
                        down(l * (2 * NC) + j * SLOTS + (n0 + i), i, False, False)
                for c in range((ROUNDS - 1) * SLOTS + 1, NC):
                    if c + 1 < NC:
                        up(l * (2 * NC) + (n0 + c + 1), c + 1, landed(l, use0 + c + 1))
                    down(l * (2 * NC) + (n0 + c), c, False, c == NC - 1)

            def norm(l, name):
                columns(l, name)
                turned(l, name)
                for n in (0, 2):
                    pe.wait_ge(*AC.at(l, name + f" hT {n}"))
                for n in (1, 3):
                    pe.wait_ge(*DV.at(l, name + f" hT {n}"))

            def window_summed(l, window):
                pe.wait_ge(ada_done, l * (8 * ADA_LAYER) + 8 * (ADA_PRE + (window + 1) * ADA_WINDOW))

            pe.wait_ge(small_full, 32)
            pe.wait_ge(*PO.at(None, "ident"))
            turn(ps[:, 4, 0:8], rows_a[0:8, :]).then_inc(*PE.step("c columns"))
            pe.wait_ge(*PO.at(None, "eps"))
            pe.wait_ge(*AC.at(None, "cond"))
            PE.next_part()
            with pe.Fori(0, DEPTH) as l:
                pe.wait_ge(params_full, l * (16 * N_PARAM_DMAS) + 16 * N_PARAM_DMAS)
                turn(ps[:, 4, 0:ROWS_A], rows_a[0:ROWS_A, :])
                turn(ps[:, 4, 128:128 + ROWS_B], rows_b[0:ROWS_B, :]).then_inc(*PE.step("params"))
                pe.wait_ge(ada_done, l * (8 * ADA_LAYER) + 8 * ADA_PRE)
                pe.wait_ge(*AC.at(l, "params"))
                norm(l, "norm 0")
                ffn(l, 0, "half 0")
                window_summed(l, 0)
                gate(l, "half 0", R_ADA + 16)
                pe.wait_ge(*DV.at(l, "half 0 Y read"))
                norm(l, "norm 1")
                pe.wait_ge(*PO.at(None, "constants"))

                owed = [False]

                def block_of(b):
                    use = NC + b
                    pe.wait_ge(*landed(l, use))
                    wide = sum(w for _, w in PROJ[b])
                    return view(ring[:, SLOT_OF[use], 0:8 * wide], 8, wide)

                def product(out_, w, cols, tokens=None):
                    for k in range(KT):
                        if tokens is None:
                            last = mm(out_, w[:, k, cols], hT[:, k, :], start=(k == 0), stop=(k == KT - 1))
                        else:
                            last = mm(out_, hT[:, k, tokens], w[:, k, cols], start=(k == 0), stop=(k == KT - 1))
                        if k == 0 and owed[0]:
                            last.then_inc(slot_free, 1)
                            owed[0] = False
                    return last

                for b in range(4):
                    w = block_of(b)
                    for n in range(3):
                        i = 3 * b + n
                        last = product(duo(i // 2)[:, i % 2, :], w, slice(n * P, n * P + P))
                        if i % 2:
                            last.then_inc(*PE.step(f"proj {i // 2}"))
                    owed[0] = True
                w = block_of(4)
                product(ps[0:64, 6, 0:256], w, slice(0, 64))
                product(ps[0:96, 6, 256:512], w, slice(64, 160)).then_inc(*PE.step("low rank"))
                product(ps[0:4, 7, 0:256], w, slice(160, 164))
                product(ps[0:4, 7, 256:512], w, slice(164, 168)).then_inc(*PE.step("i f"))
                at = 168
                for i in range(8):
                    if i in (1, 4, 7):
                        owed[0] = True
                        w, at = block_of({1: 5, 4: 6, 7: 7}[i]), 0
                    if i % 2 == 0:
                        pe.wait_ge(*AC.at(l, f"proj {i // 2}"))
                    last = product(duo(i // 2)[:, i % 2, :], w, slice(at, at + P))
                    at += P
                    if i % 2:
                        last.then_inc(*PE.step(f"qk {i // 2}"))
                for half in range(2):
                    for t in range(TT):
                        if half == 0:
                            pe.wait_ge(*AC.at(l, f"proj {4 + t}"))
                        last = product(ps[:, 4 + t, half * 256:half * 256 + 256], w, slice(at, at + 256),
                                       slice(t * P, t * P + P))
                        if half:
                            last.then_inc(*PE.step(f"v {t}"))
                    if half == 0:
                        owed[0] = True
                        w, at = block_of(8), 0
                at = 256
                for i in range(4):
                    if i == 1:
                        owed[0] = True
                        w, at = block_of(9), 0
                    if i == 0:
                        pe.wait_ge(*AC.at(l, "low rank"))
                    if i == 2:
                        pe.wait_ge(*AC.at(l, "i f"))
                    last = product(duo(6 + i // 2)[:, i % 2, :], w, slice(at, at + P))
                    at += P
                    if i % 2:
                        last.then_inc(*PE.step(f"o {i // 2}"))
                li, fp, fa, lf, b_, c_, m_, nm, en, wg, im = range(11)
                R = rows_m[0:4]

                def head_rows(h):
                    return ident[0:4, h:h + 1].broadcast_to([4, P])

                pe.wait_ge(*DV.at(l, "m rows"))
                pe.wait_ge(*AC.at(l, "qk 3"))
                for h in range(NH):
                    last = mm(duo(2 + h // 2)[:, h % 2, :], head_rows(h), R[:, nm, :])
                    if h == 0:
                        last.then_inc(slot_free, 1)
                last.then_inc(*PE.step("m spread"))
                pe.wait_ge(*AC.at(l, "m exps"))
                pe.wait_ge(*DV.at(l, "v 1"))
                for n, (row, c) in enumerate(((c_, 0), (c_, 1), (en, 0), (en, 1), (wg, 0))):
                    last = mm(ps[:, 4, 4 * n:4 * n + 4], R[:, row, c * P:c * P + P], ident[0:4, 0:4])
                last.then_inc(*PE.step("m columns"))
                pe.wait_ge(*AC.at(l, "qk ready"))
                for c in range(2):
                    for h in range(NH):
                        last = mm(quad(c)[:, h, :], qk[:, 4 + h, c * P:c * P + P], qk[:, h, c * P:c * P + P])
                    last.then_inc(*PE.step(f"scores {c}"))
                for h in range(NH):
                    last = turn(quad(5)[:, h, :], qk[:, 4 + h, 0:P])
                last.then_inc(*PE.step("k turned"))
                pe.wait_ge(*DV.at(l, "cols_m"))
                for h in range(NH):
                    last = mm(quad(4)[:, h, :], head_rows(h), R[:, im, P:T])
                last.then_inc(*PE.step("inter spread"))
                pe.wait_ge(*AC.at(l, "wk"))
                for h in range(NH):
                    if h == 2:
                        pe.wait_ge(*DV.at(l, "q_in"))
                    last = mm(duo(5 - h // 2)[:, h % 2, 0:129], wk[:, h, :], v_aug[:, 0, h, :])
                    if h % 2:
                        last.then_inc(*PE.step(f"state {h // 2}"))
                pe.wait_ge(*DV.at(l, "weights 1"))
                pe.wait_ge(*AC.at(l, "state 1"))
                for i in range(8):
                    c, h = divmod(i, NH)
                    dst = ps[:, i // 2, (i % 2) * 256:(i % 2) * 256 + 129]
                    last = mm(dst, e_t[:, i, :], v_aug[:, c, h, :], stop=(c == 0))
                    if c:
                        last = mm(dst, q_in[:, h, :], c_aug[:, h, :], start=False)
                last.then_inc(*PE.step("num"))

                def r_up(p):
                    mm(ps[:, 4, 0:256], up_wa[:, 0, p * P:p * P + P], low_wa[:, :])
                    mm(ps[:, 4, 256:512], up_wa[:, 1, p * P:p * P + P], low_wa[:, :])\
                        .then_inc(*PE.step(f"up {p}"))

                pe.wait_ge(*AC.at(l, "tanh"))
                pe.wait_ge(*DV.at(l, "low rank shifted"))
                r_up(0)
                pe.wait_ge(*DV.at(l, "m normed"))
                for h in range(NH):
                    for c in range(2):
                        last = turn(duo(h // 2)[:, h % 2, c * P:c * P + P], yn_m[:, c, h * P:h * P + P])
                    if h % 2:
                        last.then_inc(*PE.step(f"y_m {h // 2}"))

                for g in range(2):
                    for q in range(2):
                        p = 2 * g + q
                        if p:
                            pe.wait_ge(*(AC.at(l, f"sigmoids {p - 1}") if q else DV.at(l, "y 0")))
                            r_up(p)
                        pe.wait_ge(*AC.at(l, f"kk squared {p}"))
                        mm(ps[:, 5, 0:256], headsum[:, :], sq).then_inc(*PE.step(f"kk norm {p}"))
                        pe.wait_ge(*DV.at(l, f"bonus weights {p}"))
                        mm(ps[:, 7, 256:512], headsum[:, :], kk).then_inc(*PE.step(f"bonus {p}"))
                        if p == 0:
                            pe.wait_ge(*DV.at(l, "y_m"))
                        pe.wait_ge(*DV.at(l, f"a r {p}"))
                        if q:
                            pe.wait_ge(*AC.at(l, f"turned {p - 1} 1"))
                        for t in range(TT):
                            turn(ps[:, 0, t * P:t * P + P], raw[:, 8 + p, 1 + t * P:1 + t * P + P])
                        for t in range(TT):
                            last = turn(ps[:, 0, 256 + t * P:256 + t * P + P], ar[:, q, t, 0, :])
                        last.then_inc(*PE.step(f"turned {p} 0"))
                        pe.wait_ge(*DV.at(l, f"hats {p}"))
                        for n in range(2):
                            for t in range(TT):
                                last = turn(ps[:, 1, n * 256 + t * P:n * 256 + t * P + P],
                                            hats[:, q, n, t * P:t * P + P])
                        last.then_inc(*PE.step(f"turned {p} 1"))
                    instances = [(4 * q + 2 * t + h, q, t, slice(64 * h, 64 * h + 64))
                                 for q in range(2) for t in range(TT) for h in range(2)]
                    pe.wait_ge(*DV.at(l, f"prep {2 * g + 1}"))
                    pe.wait_ge(*AC.at(l, f"turned {2 * g + 1} 1"))
                    for i, q, t, hh in instances:
                        tok = slice(t * P, t * P + P)
                        if i >= 4:
                            pe.wait_ge(*DV.at(l, f"m_t {g} {i - 4}"))
                        mm(ps[:, i % 4, 0:256], bt[hh, q, tok], ar[hh, q, t, :, :])
                        mm(ps[:, i % 4, 256:512], kt[hh, q, tok], ar[hh, q, t, :, :])\
                            .then_inc(*PE.step(f"m_t {g} {i}"))
                    for h in range(2):
                        for i, q, t, hh in instances[h::2]:
                            last = mm(quad(4 + h)[:, i // 2, :], ar[hh, q, t, 0, :], bt[hh, q, t * P:t * P + P])
                        last.then_inc(*PE.step(f"m_n {g} {h}"))

                    def batch(label, n, bank, lhsT, rhs, waits):
                        for w in waits:
                            pe.wait_ge(*w)
                        for i in range(4 * n, 4 * n + 4):
                            if rhs is None:
                                last = turn(quad(3 * n + bank)[:, i % 4, :], lhsT(i))
                            else:
                                last = mm(quad(3 * n + bank)[:, i % 4, :], lhsT(i), rhs(i))
                        last.then_inc(*PE.step(f"{label} {g} {n}"))

                    def of(tile):
                        return lambda i: tile[:, i, :]
                    nt, mrb, mak, mrk = (of(m_t[:, :, m, :]) for m in range(4))
                    n16, o32, o64 = (of(m_n[:, m, :, :]) for m in range(3))
                    P2, P2T, XT = of(p2), of(p2t), of(xt)
                    pe.wait_ge(*DV.at(l, f"m_t {g} 7"))
                    for i, q, t, hh in instances:
                        last = mm(view(ps[:, 6, :], 8, 64)[:, i, :], mak(i), v_tm[:, q, t, hh])
                    last.then_inc(*PE.step(f"z0 {g}"))
                    for n in range(2):
                        batch("p2", n, 0, nt, n16, [DV.at(l, f"m_n {g} 1")])
                        batch("p2t", n, 1, n16, nt, [])
                    for n in range(2):
                        batch("p4", n, 0, P2T, P2, [DV.at(l, f"p2 {g} {n}"), AC.at(l, f"p2t {g} {n}")])
                        batch("xt 2", n, 2, P2, XT, [DV.at(l, f"xt 1 {g} {n}")])
                        batch("p4t", n, 1, P2, P2T, [])
                    for n in range(2):
                        batch("p8", n, 0, nt, n16, [DV.at(l, f"p4 {g} {n}"), AC.at(l, f"p4t {g} {n}")])
                        batch("xt 4", n, 2, n16, XT, [DV.at(l, f"xt 2 {g} {n}")])
                    for n in range(2):
                        batch("xt 8", n, 2, P2, XT, [AC.at(l, f"p8 {g} {n}"), DV.at(l, f"xt 4 {g} {n}")])
                    for size, before, off in ((32, "xt 8", o32), (64, "xt 32", o64)):
                        for n in range(2):
                            batch(f"x{size}", n, 0, XT, None, [DV.at(l, f"{before} {g} {n}")])
                            batch(f"g{size}", n, 1, off, XT, [])
                        for n in range(2):
                            batch(f"xt {size}", n, 2, P2T, P2, [AC.at(l, f"x{size} {g} {n}"),
                                                                DV.at(l, f"g{size} {g} {n}")])
                    for n in range(2):
                        batch("uz", n, 0, XT, of(az), [DV.at(l, f"xt 64 {g} {n}"), AC.at(l, f"z0 {g}")])
                    pe.wait_ge(*AC.at(l, f"uz {g} 1"))
                    for i, q, t, hh in instances:
                        last = mm(quad(1)[hh, 2 * q + t, :], uz[:, i, 0:64], mrb(i))
                    last.then_inc(*PE.step(f"qt {g}"))

                    def chunks(i, t, first, end):
                        for c in range(max(2 * t, first), min(2 * t + 2, end)):
                            yield c, slice(64 * (c % 2), 64 * (c % 2) + 64)
                    for i, q, t, hh in instances:
                        for c, cc in chunks(i, t, 1, 3):
                            last = mm(ps[hh, 1 + c, 64 * q:64 * q + 64], uz[cc, i, 0:64],
                                      b_tm[cc, q, t, hh])
                    last.then_inc(*PE.step(f"gt {g}"))
                    for i, q, t, hh in instances:
                        for c, cc in chunks(i, t, 0, 3):
                            at = 64 * (q + 2 * (c // 2))
                            dst = ps[hh, 4 + c % 2, at:at + 64]
                            mm(dst, b_tm[cc, q, t, hh], uz[cc, i, 64:128], stop=False)
                            last = mm(dst, k_tm[cc, q, t, hh], v_tm[cc, q, t, hh], start=False)
                    last.then_inc(*PE.step(f"h {g}"))

                    def state(q, c):
                        return h_s[:, 3 * q, :] if c == 1 else s_s[:, 2 * q + c - 2, :]

                    def y_of(i):
                        q, t, h = i // 4, i // 2 % 2, i % 2
                        return ps[:, 7 * h, (2 * t + q) * 64:(2 * t + q) * 64 + 64]

                    def y_local(some):
                        for i, q, t, hh in some:
                            mm(y_of(i), mrb(i), uz[:, i, 64:128], start=i < 2, skip_group_check=True)
                            mm(y_of(i), mrk(i), v_tm[:, q, t, hh], start=False, skip_group_check=True)
                    pe.wait_ge(*AC.at(l, f"h {g}"))
                    pe.wait_ge(*DV.at(l, f"gt {g}"))
                    for c in (1, 2):
                        if c == 2:
                            pe.wait_ge(*DV.at(l, f"chain {g} 1"))
                        y_local(instances[3 * c - 3:3 * c])
                        for q in range(2):
                            for h in range(2):
                                hh = slice(64 * h, 64 * h + 64)
                                at = 128 * (c - 1) + 64 * q
                                last = mm(ps[hh, 6, at:at + 64], gt_s[hh, 2 * q + c - 1, :], state(q, c)[hh, :])
                        last.then_inc(*PE.step(f"chain {g} {c}"))
                    pe.wait_ge(*DV.at(l, f"chain {g} 2"))
                    y_local(instances[6:8])
                    for i, q, t, hh in instances:
                        for c, cc in chunks(i, t, 1, 4):
                            last = mm(y_of(i)[cc, :], qt[hh, 2 * q + t, cc], state(q, c)[hh, :],
                                      start=False, stop=True, skip_group_check=True)
                    last.then_inc(*PE.step(f"y {g}"))

                pe.wait_ge(*AC.at(l, "low g"))
                for b in range(2):
                    for p in (2 * b, 2 * b + 1):
                        last = mm(duo(2 + b)[:, p % 2, :], up_g[:, p * P:p * P + P], low_g[:, :])
                    last.then_inc(*PE.step(f"g {b}"))
                pe.wait_ge(*DV.at(l, "r normed"))
                for b in range(2):
                    for p in (2 * b, 2 * b + 1):
                        for t in range(TT):
                            last = turn(duo(b)[:, p % 2, t * P:t * P + P], yn_r[:, t, p * P:p * P + P])
                    last.then_inc(*PE.step(f"y turned {b}"))

                for ct in range(KT):
                    use = NC + N_PROJ + ct
                    slot = ring[:, SLOT_OF[use], :]
                    pe.wait_ge(*landed(l, use))
                    if ct >= 2:
                        pe.wait_ge(*AC.at(l, f"gates {ct - 2}"))
                    for n in range(2):
                        last = product(duo(4 + ct % 2)[:, n, :], view(slot[:, n * 1024:n * 1024 + 1024], 8, P),
                                       slice(0, P))
                    last.then_inc(*PE.step(f"gates {ct}"))
                    if ct == 0:
                        pe.wait_ge(*DV.at(l, "y_r"))
                    if ct >= 2:
                        pe.wait_ge(*DV.at(l, f"merged {ct - 2}"))
                    for n, y in enumerate((y_r, y_m)):
                        for k in range(4):
                            last = mm(duo(6 + ct % 2)[:, n, :],
                                      view(slot[:, 2048 + n * 512:2560 + n * 512], 4, P)[:, k, :], y[:, k, :],
                                      start=(k == 0), stop=(k == 3))
                    last.then_inc(*PE.step(f"branches {ct}"))
                    owed[0] = True
                for k in range(KT):
                    use = NC + N_PROJ + N_MERGE + k // 2
                    if k % 2 == 0:
                        pe.wait_ge(*landed(l, use))
                    pe.wait_ge(*DV.at(l, f"merge {k}"))
                    for t in range(TT):
                        for m in range(2):
                            at = (k % 2) * D + m * 512
                            last = mm(ps[:, 2 * t + m, :], merged[:, k, t * P:t * P + P],
                                      ring[:, SLOT_OF[use], at:at + 512], start=(k == 0), stop=(k == KT - 1))
                            if t == m == 0 and owed[0]:
                                last.then_inc(slot_free, 1)
                                owed[0] = False
                    owed[0] = k % 2 == 1
                last.then_inc(*PE.step("mixer Y"))
                window_summed(l, 1)
                pe.wait_ge(*DV.at(l, "merged 7"))
                gate(l, "mixer", R_ADA + 40, owed)
                pe.wait_ge(*DV.at(l, "mixer Y read"))
                norm(l, "norm 2")
                ffn(l, 1, "half 1")
                window_summed(l, 2)
                gate(l, "half 1", R_ADA + 64)
                pe.wait_ge(*DV.at(l, "half 1 Y read"))
            PE.next_part()
            PE.close()


_INS = ["x", "c", "ada_w", "ada_b", "norm_g", "ffn_w_in", "ffn_w_out", "mix_w_in", "rwkv_mu", "rwkv_w0",
        "rwkv_w_up", "rwkv_a0", "rwkv_a_up", "rwkv_g_up", "rwkv_k_k", "rwkv_k_a", "rwkv_r_k", "rwkv_ln_g",
        "rwkv_ln_b", "mlstm_conv_w", "mlstm_conv_b", "mlstm_gate_b", "mlstm_ln_g", "branch_w_rwkv",
        "branch_w_mlstm", "mix_w_out", "final_g"]


def kernel(**inputs):
    import concourse.bacc as _bacc
    from concourse.bass_utils import run_bass_kernel_spmd as _run

    arrays = {f"in_{name}_dram": np.ascontiguousarray(inputs[name]) for name in _INS}
    numbers = {}
    for _ in range(2):
        nc = _bacc.Bacc("TRN2", target_bir_lowering=False, num_devices=1)
        args = [nc.dram_tensor(name, a.shape, mybir.dt.from_np(a.dtype), kind="ExternalInput").ap()
                for name, a in arrays.items()]
        args.append(nc.dram_tensor("out_dram", (1, T, D), F32, kind="ExternalOutput").ap())
        trunk(nc, numbers, *args)
    r = _run(nc, [arrays], core_ids=[0])
    return r.results[0]["out_dram"]
```
